# Optimizing a Trainium2 kernel written in Bass

```python
import math
import jax
import jax.numpy as jnp
from jax import lax
import numpy as np

D_MODEL = 2048
BATCH = 1
SEQ = 512
DEPTH = 1

HEAD_DIM = D_MODEL // 16
N_HEADS_MOBA = 6
N_HEADS_FOX = 6
N_HEADS_MEM = 4
W_MOBA = N_HEADS_MOBA * HEAD_DIM
W_FOX = N_HEADS_FOX * HEAD_DIM
W_MEM = N_HEADS_MEM * HEAD_DIM
MIX_WIDTH = W_MOBA + W_FOX + W_MEM
IN_WIDTH = 4 * W_MOBA + 4 * W_FOX + N_HEADS_FOX + 2 * W_MEM
N_MEM = 256
MOBA_BLOCK = 256
MOBA_TOPK = 3
MOBA_Q_CHUNK = 16
FOX_Q_BLOCK = 128
T5_BUCKETS = 32
T5_MAX_DIST = 128
EPS = 1e-6
NEG = -1e30

kernel_name = "hybrid_moba_fox_memory_parallel_heads"

def rms_norm(x, g):
    xf = x.astype(jnp.float32)
    y = xf * lax.rsqrt(jnp.mean(xf * xf, axis=-1, keepdims=True) + EPS)
    return (y * g.astype(jnp.float32)).astype(x.dtype)

def split_heads(t, n_heads):
    b, s, _ = t.shape
    return t.reshape(b, s, n_heads, HEAD_DIM).transpose(0, 2, 1, 3)

def merge_heads(t):
    b, h, s, d = t.shape
    return t.transpose(0, 2, 1, 3).reshape(b, s, h * d)

def t5_bucket(dist):
    n = jnp.maximum(dist, 0)
    max_exact = T5_BUCKETS // 2
    nf = jnp.maximum(n, 1).astype(jnp.float32)
    large = max_exact + (jnp.log(nf / max_exact) / math.log(T5_MAX_DIST / max_exact)
                         * (T5_BUCKETS - max_exact)).astype(jnp.int32)
    large = jnp.minimum(large, T5_BUCKETS - 1)
    return jnp.where(n < max_exact, n, large)

def in_splits():
    sizes = [W_MOBA] * 4 + [W_FOX] * 4 + [N_HEADS_FOX] + [W_MEM] * 2
    return [int(v) for v in np.cumsum(sizes)[:-1]]

def moba_attention(q, k, v, rel_bias):
    b, h, s, dh = q.shape
    nb = -(-s // MOBA_BLOCK)
    pad = nb * MOBA_BLOCK - s
    k_blk = jnp.pad(k, ((0, 0), (0, 0), (0, pad), (0, 0))).reshape(b, h, nb, MOBA_BLOCK, dh)
    v_blk = jnp.pad(v, ((0, 0), (0, 0), (0, pad), (0, 0))).reshape(b, h, nb, MOBA_BLOCK, dh)
    k_mean = jnp.mean(k_blk.astype(jnp.float32), axis=3)
    scale = dh ** -0.5
    kk = max(min(MOBA_TOPK, nb - 1), 1)
    q_blk_id = jnp.arange(s) // MOBA_BLOCK
    gate = jnp.einsum('bhsd,bhnd->bhsn', q, k_mean.astype(q.dtype),
                      preferred_element_type=jnp.float32)
    past = jnp.arange(nb)[None, :] < q_blk_id[:, None]
    gate = jnp.where(past, gate, NEG)
    _, sel = lax.top_k(gate, kk)
    sel_valid = sel < q_blk_id[:, None]

    n_chunks = s // MOBA_Q_CHUNK
    q_c = q.reshape(b, h, n_chunks, MOBA_Q_CHUNK, dh).transpose(2, 0, 1, 3, 4)
    sel_c = sel.reshape(b, h, n_chunks, MOBA_Q_CHUNK, kk).transpose(2, 0, 1, 3, 4)
    val_c = sel_valid.reshape(b, h, n_chunks, MOBA_Q_CHUNK, kk).transpose(2, 0, 1, 3, 4)
    starts = jnp.arange(n_chunks, dtype=jnp.int32) * MOBA_Q_CHUNK
    b_idx = jnp.arange(b)[:, None, None, None]
    h_idx = jnp.arange(h)[None, :, None, None]
    h_idx5 = h_idx[..., None]
    blk_off = jnp.arange(MOBA_BLOCK)

    def chunk_fn(args):
        qc, selc, validc, start = args
        tq = start + jnp.arange(MOBA_Q_CHUNK)
        own = start // MOBA_BLOCK
        k_own = lax.dynamic_index_in_dim(k_blk, own, axis=2, keepdims=False)
        v_own = lax.dynamic_index_in_dim(v_blk, own, axis=2, keepdims=False)
        dist_own = tq[:, None] - (own * MOBA_BLOCK + blk_off)[None, :]
        l_own = jnp.einsum('bhqd,bhkd->bhqk', qc, k_own,
                           preferred_element_type=jnp.float32) * scale
        l_own = l_own + rel_bias[:, t5_bucket(dist_own)]
        l_own = jnp.where(dist_own >= 0, l_own, NEG)
        k_sel = k_blk[b_idx, h_idx, selc]
        v_sel = v_blk[b_idx, h_idx, selc]
        l_sel = jnp.einsum('bhqd,bhqnkd->bhqnk', qc, k_sel,
                           preferred_element_type=jnp.float32) * scale
        dist_sel = tq[None, None, :, None, None] - (selc[..., None] * MOBA_BLOCK + blk_off)
        l_sel = l_sel + rel_bias[h_idx5, t5_bucket(dist_sel)]
        l_sel = jnp.where(validc[..., None], l_sel, NEG)
        l_sel = l_sel.reshape(b, h, MOBA_Q_CHUNK, kk * MOBA_BLOCK)
        p = jax.nn.softmax(jnp.concatenate([l_sel, l_own], axis=-1), axis=-1).astype(v.dtype)
        out = jnp.einsum('bhqm,bhqmd->bhqd', p[..., :kk * MOBA_BLOCK],
                         v_sel.reshape(b, h, MOBA_Q_CHUNK, kk * MOBA_BLOCK, dh))
        out = out + jnp.einsum('bhqk,bhkd->bhqd', p[..., kk * MOBA_BLOCK:], v_own)
        return out.astype(q.dtype)

    out = lax.map(chunk_fn, (q_c, sel_c, val_c, starts))
    return out.transpose(1, 2, 0, 3, 4).reshape(b, h, s, dh)

def forgetting_attention(q, k, v, log_f):
    b, h, s, dh = q.shape
    c = jnp.cumsum(log_f, axis=-1)
    n_blk = s // FOX_Q_BLOCK
    q_c = q.reshape(b, h, n_blk, FOX_Q_BLOCK, dh).transpose(2, 0, 1, 3, 4)
    c_c = c.reshape(b, h, n_blk, FOX_Q_BLOCK).transpose(2, 0, 1, 3)
    starts = jnp.arange(n_blk, dtype=jnp.int32) * FOX_Q_BLOCK
    kpos = jnp.arange(s)
    scale = dh ** -0.5

    def blk_fn(args):
        qb, cb, start = args
        tq = start + jnp.arange(FOX_Q_BLOCK)
        l = jnp.einsum('bhqd,bhkd->bhqk', qb, k, preferred_element_type=jnp.float32) * scale
        l = l + cb[..., None] - c[:, :, None, :]
        l = jnp.where(kpos[None, :] <= tq[:, None], l, NEG)
        p = jax.nn.softmax(l, axis=-1).astype(v.dtype)
        return jnp.einsum('bhqk,bhkd->bhqd', p, v)

    out = lax.map(blk_fn, (q_c, c_c, starts))
    return out.transpose(1, 2, 0, 3, 4).reshape(b, h, s, dh)

def memory_attention(q, k, v):
    l = jnp.einsum('bhqd,bhmd->bhqm', q, k, preferred_element_type=jnp.float32) * (HEAD_DIM ** -0.5)
    p = jax.nn.softmax(l, axis=-1).astype(v.dtype)
    return jnp.einsum('bhqm,bhmd->bhqd', p, v)

def setup_inputs(seed: int = 0) -> dict:
    key = jax.random.key(seed)
    ks = jax.random.split(key, 11)
    f32 = jnp.float32
    x = jax.random.normal(ks[0], (BATCH, SEQ, D_MODEL), f32)
    mem = jax.random.normal(ks[1], (BATCH, N_MEM, D_MODEL), f32)
    w_in = jax.random.normal(ks[2], (DEPTH, D_MODEL, IN_WIDTH), f32) * D_MODEL ** -0.5
    b_forget = 2.0 + 0.5 * jax.random.normal(ks[3], (DEPTH, N_HEADS_FOX), f32)
    w_mem_kv = jax.random.normal(ks[4], (DEPTH, D_MODEL, 2 * W_MEM), f32) * D_MODEL ** -0.5
    w_out = jax.random.normal(ks[5], (DEPTH, MIX_WIDTH, D_MODEL), f32) * MIX_WIDTH ** -0.5
    g_pre = 1.0 + 0.1 * jax.random.normal(ks[6], (DEPTH, D_MODEL), f32)
    g_post = 1.0 + 0.1 * jax.random.normal(ks[7], (DEPTH, D_MODEL), f32)
    g_mem = 1.0 + 0.1 * jax.random.normal(ks[8], (DEPTH, D_MODEL), f32)
    rel_bias = 0.5 * jax.random.normal(ks[9], (N_HEADS_MOBA, T5_BUCKETS), f32)
    return {"x": x, "mem": mem, "w_in": w_in, "b_forget": b_forget, "w_mem_kv": w_mem_kv,
            "w_out": w_out, "g_pre": g_pre, "g_post": g_post, "g_mem": g_mem,
            "rel_bias": rel_bias}

def reference(x, mem, w_in, b_forget, w_mem_kv, w_out, g_pre, g_post, g_mem, rel_bias):
    for layer in range(DEPTH):
        h = rms_norm(x, g_pre[layer])
        proj = jnp.einsum('bsd,de->bse', h, w_in[layer])
        qa, ka, va, ga, qb, kb, vb, gb, fb, qm, gm = jnp.split(proj, in_splits(), axis=-1)
        out_a = moba_attention(split_heads(qa, N_HEADS_MOBA), split_heads(ka, N_HEADS_MOBA),
                               split_heads(va, N_HEADS_MOBA), rel_bias)
        log_f = jax.nn.log_sigmoid((fb + b_forget[layer]).astype(jnp.float32)).transpose(0, 2, 1)
        out_b = forgetting_attention(split_heads(qb, N_HEADS_FOX), split_heads(kb, N_HEADS_FOX),
                                     split_heads(vb, N_HEADS_FOX), log_f)
        mkv = jnp.einsum('bmd,de->bme', rms_norm(mem, g_mem[layer]), w_mem_kv[layer])
        km, vm = jnp.split(mkv, 2, axis=-1)
        out_m = memory_attention(split_heads(qm, N_HEADS_MEM), split_heads(km, N_HEADS_MEM),
                                 split_heads(vm, N_HEADS_MEM))
        y = jnp.concatenate([merge_heads(out_a) * jax.nn.silu(ga),
                             merge_heads(out_b) * jax.nn.silu(gb),
                             merge_heads(out_m) * jax.nn.silu(gm)], axis=-1)
        o = jnp.einsum('bse,ed->bsd', y, w_out[layer])
        x = x + rms_norm(o, g_post[layer])
    return x


_drawn_inputs = setup_inputs


def setup_inputs(seed=0):
    import zlib

    import numpy as np

    out = dict(_drawn_inputs(seed))
    spreads = {}
    factors = {'g_mem': 2.897}
    for name, (base, spread) in spreads.items():
        noise = np.random.default_rng([zlib.crc32(name.encode()), seed]).standard_normal(out[name].shape)
        drawn = base * np.exp(spread * noise) if base else spread * noise
        out[name] = jnp.asarray(drawn.astype(out[name].dtype))
    for name, factor in factors.items():
        out[name] = (out[name] * factor).astype(out[name].dtype)
    return out
```

```python
import math
from contextlib import ExitStack

import numpy as np

import concourse.bass as bass
from concourse import mybir

F32 = mybir.dt.float32
F32R = mybir.dt.float32r
BF16 = mybir.dt.bfloat16
ALU = mybir.AluOpType
ACTF = mybir.ActivationFunctionType
AX_X = mybir.AxisListType.X

P = 128
D = 2048
S = 512
KT = D // P
QB = S // P
NMEM = 256
MB = NMEM // P
DH = 128
NA, NB, NM = 6, 6, 4
NAB = NA + NB
NH = NAB + NM
WG = NA * DH
SCALE = DH ** -0.5
EPS = 1e-6
NEG = -1e30
BIG = 3e38
BUCKETS, MAX_DIST = 32, 128
TABLE = 640

COL_F = 8 * WG
COL_QM = COL_F + NB
COL_GM = COL_QM + NM * DH

RING = 4
PIECE_KT = KT // 2
PW = PIECE_KT * P
STRIPS_MEM = 2 * NM
STRIPS = STRIPS_MEM + 2 * NM + 4 * NAB
PIECES = 2 * STRIPS
OCH = D // 512
OPC = NH // 2
TILES = MB + QB
PAIRS = TILES // 2
LOAD_DURING = {1: 2, 2: 3, 3: 4, 4: 5}
SQUARE_DURING = {0: 2, 1: 3, 2: 4, 3: 5}
SCALE_DURING = {1: 2, 2: 3, 3: 4, 4: 5}
TURN_DURING = {3: (1, 0), 4: (1, 1), 5: (2, 0), 6: (2, 1)}
POOL_PIECES = [0, 1, 2, 3, 4, 5, 7, 8, 9, 10, 11, 13, 15]
WARM_UP = 12
SERIES = [1.0 / (2 * k + 1) for k in range(8, 0, -1)]
LOW_AT = [P * i * (i + 1) // 2 for i in range(QB - 1)]
MASK_PARTS = QB + QB - 2
OUT_SLOT = [0, 1, 4, 5, 2, 3, 6, 7]


def lo_count(n):
    if isinstance(n, int) and n < 2 * STRIPS_MEM:
        pool = n in POOL_PIECES
        return pool, sum((i in POOL_PIECES) == pool for i in range(n + 1))
    return False, n + 1 - len(POOL_PIECES)


def bucket_rows():
    dist = S - 1 - np.arange(TABLE)
    exact = BUCKETS // 2
    n = np.maximum(dist, 1).astype(np.float32)
    large = exact + (np.log(n / exact) / math.log(MAX_DIST / exact) * (BUCKETS - exact)).astype(np.int32)
    b = np.where(dist < exact, np.maximum(dist, 0), np.minimum(large, BUCKETS - 1))
    hot = (b[None, :] == np.arange(BUCKETS)[:, None]) & (dist >= 0)[None, :]
    return np.concatenate([hot, NEG * (dist < 0)[None, :]]).astype(np.float32)


class MHead:

    def __init__(self, m):
        self.m, self.hh, self.scores, self.pt, self.y_tile = m, m, 2 * m, 2 * m, NAB + m
        self.memory, self.v = True, m
        self.strip_q = STRIPS_MEM + 2 * m
        self.strip_g = self.strip_q + 1


class ABHead:

    def __init__(self, a):
        self.a, self.hh, self.scores, self.pt, self.y_tile = a, NM + a, 2 * NM + 4 * a, 2 * NM + 3 * a, a
        self.memory, self.v = False, NM + a
        self.strip_q = STRIPS_MEM + 2 * NM + 4 * a
        self.strip_k, self.strip_v, self.strip_g = self.strip_q + 1, self.strip_q + 2, self.strip_q + 3


def build(nc, x, mem, w_in, b_forget, w_mem_kv, w_out, g_pre, g_post, g_mem, rel_bias, buckets, out):
    ctx = ExitStack()
    with ctx:
        base = [(nc.sbuf_base + 31) // 32 * 32]

        def place(name, shape, dt, at=None):
            off = base[0] if at is None else at
            t = nc.alloc_sbuf_tensor_at(name, shape, dt, offset=off)
            if at is None:
                base[0] = off + (4 * int(np.prod(shape[1:])) + 31) // 32 * 32
            return t, off

        xT, _ = place("xT", [P, 2, KT, S], F32R)
        y, y_at = place("y", [P, 2, NH, S], F32R)
        raw, _ = place("raw", [P, RING, PW], F32)
        ring, ring_at = place("ring", [P, RING, 2, PW], F32R)
        q, ws_at = place("q", [P, 2, S], F32R)
        prob, _ = place("prob", [P, 2, S], F32)
        kv, _ = place("kv", [P, 4 * S], F32R)
        pT, _ = place("pT", [P, 2, QB, S], F32R)
        bias, bias_at = place("bias", [P, S], F32)
        ybuf, ybuf_at = place("ybuf", [P, S], F32)
        gate, _ = place("gate", [P, S], F32)
        vT, vT_at = place("vT", [P, S], F32)
        ident, _ = place("ident", [P, P], F32)
        mask, _ = place("mask", [P, P], F32)
        bias_low, _ = place("bias_low", [P, 6 * P], F32)
        eps, _ = place("eps", [P, 1], F32)
        gains, _ = place("gains", [P, 2, KT], F32)
        relT, _ = place("relT", [BUCKETS + 1, NA], F32)
        bfor, _ = place("bfor", [NB, 1], F32)
        wf_raw, _ = place("wf_raw", [P, KT, NB], F32)
        sq, _ = place("sq", [P, 8], F32)
        part, _ = place("part", [P, QB], F32)
        stat, _ = place("stat", [P, 6, 8], F32)
        negmax, _ = place("negmax", [P, QB], F32)
        rowmax, _ = place("rowmax", [P, QB], F32)
        rowsum, _ = place("rowsum", [P, QB], F32)
        rinv, _ = place("rinv", [P, QB], F32)
        pace, _ = place("pace", [P, QB], F32)
        stage, _ = place("stage", [P, 4, D], F32, at=ws_at)
        waste, _ = place("waste", [P, D], BF16, at=ybuf_at)
        waste_mem, _ = place("waste_mem", [P, D], BF16, at=y_at + 4 * 8 * S)
        rstd_mem, _ = place("rstd_mem", [P, NMEM], F32, at=bias_at)
        rstd_diag, _ = place("rstd_diag", [P, MB, P], F32, at=bias_at + 4 * NMEM)
        ones, _ = place("ones", [P, P], F32, at=vT_at + 4 * P)
        gain_rows, _ = place("gain_rows", [KT, 2, P], F32, at=vT_at + 4 * 2 * P)
        k_mem, _ = place("k_mem", [P, NMEM], F32, at=vT_at + 4 * 2 * P)
        hot, _ = place("hot", [BUCKETS + 1, TABLE], F32, at=y_at + 4 * NAB * S)
        table, _ = place("table", [NA, TABLE], F32, at=y_at + 4 * (NH * S - TABLE))
        wf, _ = place("wf", [P, (KT + 1) * 64], F32R, at=y_at + 4 * 8 * S)
        fbuf, _ = place("fbuf", [NB, 4, S], F32, at=y_at + 4 * 8 * S)
        o_sb, _ = place("o_sb", [P, QB, D], F32, at=ring_at)
        gpost, _ = place("gpost", [P, D], F32, at=ws_at)
        xres, _ = place("xres", [P, 2, D], F32, at=ws_at + 4 * D)
        waste_o, _ = place("waste_o", [P, QB, S], F32, at=ws_at + 3 * 4 * D)

        memT = y[:, 1, :, :].rearrange("p k (a t) -> p (k a) t", a=2).rearrange("p (h k) t -> p h k t", h=2)
        kmv = y[:, 0, 0:8, :].rearrange("p k (a t) -> p (k a) t", a=2)
        wout_split = xT[:, :, :, :].rearrange("p h k s -> p (h k s)").rearrange(
            "p (n h w) -> p n h w", n=OPC, h=2)

        def pb(name):
            return ctx.enter_context(nc.psum_tensor(name, [P, S], F32))

        strip_ps = [pb("strip_ps0"), pb("strip_ps1")]
        score_ps = [pb("score_ps0"), pb("score_ps1")]
        pt_ps = [pb("pt_ps0"), pb("pt_ps1")]
        o_ps = pb("o_ps")
        vt_ps = pb("vt_ps")
        tile_ps = score_ps + pt_ps
        mem_ps = tile_ps + [o_ps, vt_ps, strip_ps[1], tile_ps[0]]
        table_banks = [(o_ps, 0, S), (vt_ps, S, TABLE)]

        table_dram = nc.dram_tensor("table_dram", [NA, TABLE], F32).ap()
        toep_dram = nc.dram_tensor("toep_dram", [NA * P, S], F32).ap()
        negc_dram = nc.dram_tensor("negc_dram", [NB, S], F32).ap()

        def sem(name):
            return ctx.enter_context(nc.semaphore(name))

        raw_landed = [sem(f"raw_landed{i}") for i in range(RING)]
        stage_landed = [sem(f"stage_landed{i}") for i in range(QB)]
        rel_landed = sem("rel_landed")
        forget_landed = sem("forget_landed")
        gain_rows_landed = sem("gain_rows_landed")
        mem_landed = [[sem(f"mem_landed{t}{h}") for h in range(2)] for t in range(MB)]
        bias_landed = sem("bias_landed")
        table_stored = sem("table_stored")
        toep_stored = sem("toep_stored")
        negc_stored = sem("negc_stored")
        gpost_landed = sem("gpost_landed")
        xres_landed = [sem("xres_landed0"), sem("xres_landed1")]
        out_stored = sem("out_stored")
        pool_consts = sem("pool_consts")
        mask_row_ready = sem("mask_row_ready")
        bias_masked = sem("bias_masked")
        hi_done = sem("hi_done")
        lo_done = sem("lo_done")
        piece_used = sem("piece_used")
        strip_free = sem("strip_free")
        squares_done = sem("squares_done")
        root_done = sem("root_done")
        stat_step = sem("stat_step")
        tile_scaled = sem("tile_scaled")
        bank_turned = sem("bank_turned")
        bank_hi = sem("bank_hi")
        bank_taken = sem("bank_taken")
        gain_turned = sem("gain_turned")
        gain_copied = sem("gain_copied")
        mem_squared = sem("mem_squared")
        diag_ready = sem("diag_ready")
        rstd_spread = sem("rstd_spread")
        k_taken = sem("k_taken")
        lo_pool = sem("lo_pool")
        part_done = sem("part_done")
        table_made = sem("table_made")
        table_copied = sem("table_copied")
        wf_cleared = sem("wf_cleared")
        wf_hi = sem("wf_hi")
        wf_ready = sem("wf_ready")
        f_done = sem("f_done")
        f_low = sem("f_low")
        f_z = sem("f_z")
        f_neg = sem("f_neg")
        f_exp = sem("f_exp")
        f_den = sem("f_den")
        f_rec = sem("f_rec")
        f_pool = sem("f_pool")
        f_parts = sem("f_parts")
        f_scan = sem("f_scan")
        q_hi = sem("q_hi")
        k_hi = sem("k_hi")
        v_turned = sem("v_turned")
        v_hi = sem("v_hi")
        v_ready = sem("v_ready")
        gate_tanh = sem("gate_tanh")
        scores_done = sem("scores_done")
        max_done = sem("max_done")
        negmax_ready = sem("negmax_ready")
        exp_done = sem("exp_done")
        rinv_ready = sem("rinv_ready")
        prob_ready = sem("prob_ready")
        pt_turned = sem("pt_turned")
        pt_hi = sem("pt_hi")
        pt_ready = sem("pt_ready")
        pv_done = sem("pv_done")
        y_raw = sem("y_raw")
        y_hi = sem("y_hi")
        y_ready = sem("y_ready")
        o_done = sem("o_done")
        out_used = sem("out_used")
        o_copied = sem("o_copied")
        o_gained = sem("o_gained")
        ssq_done = sem("ssq_done")
        final_done = sem("final_done")

        block = ctx.enter_context(nc.Block())

        w_in_v = w_in[0].rearrange("(k p) n -> p k n", p=P)
        w_kv_v = w_mem_kv[0].rearrange("(k p) n -> p k n", p=P)
        w_out_v = w_out[0].rearrange("(e p) n -> p e n", p=P)

        def token_tile(t):
            return mem[0, P * t:P * (t + 1), :] if t < MB else x[0, P * (t - MB):P * (t - MB + 1), :]

        def turn_ps(pair, b):
            return mem_ps[b] if pair == 0 else tile_ps[b % 4]

        def out_e0(p):
            return (NAB + 2 * p) % NH

        @block.sync
        def _(sp):
            def load_tile(t):
                if t == 4:
                    sp.wait_ge(bank_turned, 8)
                    sp.wait_ge(squares_done, 1)
                if t == 5:
                    sp.wait_ge(mem_squared, 1)
                sp.dma_start(stage[:, t % 4], token_tile(t)).then_inc(stage_landed[t - MB], 16)

            for i, g in enumerate((g_mem, g_pre)):
                sp.dma_start(gain_rows[:, i], g.rearrange("a (k p) -> (a k) p", p=P)).then_inc(gain_rows_landed, 16)

            def load_memory(half):
                cols = slice(D // 2 * half, D // 2 * (half + 1))
                sp.dma_start(stage[:, 1, cols], token_tile(1)[:, cols]).then_inc(mem_landed[1][half], 16)

            def load(n, slot, view, rows, col, width):
                col = col if isinstance(col, int) else sp.snap(col)
                src = view[:, rows, bass.ds(col, width)]
                if not isinstance(n, int) or n >= RING:
                    by_pool, count = lo_count(n - RING)
                    sp.wait_ge(lo_pool if by_pool else lo_done, count)
                sp.dma_start(raw[:, slot].rearrange("p (k n) -> p k n", n=src.shape[-1]), src
                             ).then_inc(raw_landed[slot], 16)

            def load_strip(t, par, view, col):
                for half in range(2):
                    if isinstance(t, int) and t == 0:
                        load_memory(half)
                    load(2 * t + half, 2 * par + half, view, slice(PIECE_KT * half, PIECE_KT * (half + 1)), col, P)

            for t in range(STRIPS_MEM):
                load_strip(t, t % 2, w_kv_v, P * t)
                if t in LOAD_DURING:
                    load_tile(LOAD_DURING[t])
                if t == 2:
                    sp.dma_start(relT[0:BUCKETS], rel_bias.rearrange("h b -> b h"),
                                 allow_slow_non_contiguous=True).then_inc(rel_landed, 16)
                    sp.dma_start(hot[:], buckets).then_inc(rel_landed, 16)
                    sp.dma_start(bfor[:], b_forget.rearrange("a h -> h a"),
                                 allow_slow_non_contiguous=True).then_inc(forget_landed, 16)
                    sp.dma_start(wf_raw[:], w_in_v[:, :, COL_F:COL_F + NB]).then_inc(forget_landed, 16)
            for m in range(NM):
                load_strip(MHead(m).strip_q, 0, w_in_v, COL_QM + P * m)
                load_strip(MHead(m).strip_g, 1, w_in_v, COL_GM + P * m)
                if m == 1:
                    sp.wait_ge(table_copied, 2)
                    sp.dma_start(table_dram, table[:]).then_inc(table_stored, 16)
                if m == 2:
                    sp.wait_ge(table_stored, 16)
                    sp.dma_start(toep_dram.rearrange("(h p) s -> h p s", h=NA),
                                 bass.AP(table_dram.tensor, P - 1, [[TABLE, NA], [-1, P], [1, S]])
                                 ).then_inc(toep_stored, 16)

            def load_head(a, forgetting):
                head = ABHead(a)
                col = P * a if not forgetting else 4 * WG - NA * P + P * a
                for j in range(4):
                    if j == 3:
                        row = a * P if isinstance(a, int) else sp.snap(a * P)
                        if not isinstance(a, int) or a > 0:
                            sp.wait_ge(negmax_ready, head.scores)
                        if forgetting:
                            src = negc_dram[bass.ds(a - NA, 1), :].partition_broadcast(P)[:, 0, :]
                        else:
                            src = toep_dram[bass.ds(row, P), :]
                        sp.dma_start(bias[:], src).then_inc(bias_landed, 16)
                    load_strip(head.strip_q + j, j % 2, w_in_v, col + WG * j)

            sp.wait_ge(toep_stored, 16)
            with sp.Fori(0, NA) as a:
                load_head(a, False)
            sp.wait_ge(f_scan, 1)
            sp.dma_start(negc_dram, fbuf[:, 1, :]).then_inc(negc_stored, 16)
            sp.wait_ge(negc_stored, 16)
            with sp.Fori(NA, NAB) as a:
                load_head(a, True)

            def load_out(c):
                for p in range(OPC):
                    e0 = out_e0(p)
                    load(PIECES + OPC * c + p, p % RING, w_out_v, slice(e0, e0 + 2), c * S, S)

            load_out(0)
            sp.wait_ge(y_ready, NH)
            sp.dma_start(gpost[:], g_post.partition_broadcast(P)[:, 0, :]).then_inc(gpost_landed, 16)
            for s in range(2):
                sp.dma_start(xres[:, s], x[0, P * s:P * (s + 1), :]).then_inc(xres_landed[s], 16)
            for c in range(1, OCH):
                load_out(c)
            for s in range(QB):
                for j in range(4):
                    sp.wait_ge(final_done, 4 * s + j + 1)
                    sp.dma_start(out[0, P * s:P * (s + 1), S * j:S * (j + 1)],
                                 o_sb[:, s, S * j:S * (j + 1)]).then_inc(out_stored, 16)
                if s + 2 < QB:
                    sp.dma_start(xres[:, s % 2], x[0, P * (s + 2):P * (s + 3), :]).then_inc(xres_landed[s % 2], 16)
            sp.wait_ge(out_stored, 16 * 4 * QB)

        @block.tensor
        def _(pe):
            def three(dst, lhs, rhs, start, stop):
                pe.matmul(dst, lhs[0], rhs[0], start=start, stop=False, skip_group_check=True)
                pe.matmul(dst, lhs[1], rhs[0], start=False, stop=False, skip_group_check=True)
                return pe.matmul(dst, lhs[0], rhs[1], start=False, stop=stop, skip_group_check=True)

            def strip(t, par, rhs, n, between=None):
                if not isinstance(t, int) or t >= 2:
                    pe.wait_ge(strip_free, t - 1)
                for half in range(2):
                    by_pool, count = lo_count(2 * t + half)
                    pe.wait_ge(lo_pool if by_pool else lo_done, count)
                    w = ring[:, 2 * par + half].rearrange("p h (k m) -> p h k m", m=P)
                    for k in range(PIECE_KT):
                        kt = PIECE_KT * half + k
                        last = three(strip_ps[par][:, 0:n], (w[:, 0, k], w[:, 1, k]), (rhs[:, 0, kt], rhs[:, 1, kt]),
                                     kt == 0, kt == KT - 1)
                    last.then_inc(piece_used, 1)
                    if half == 0 and between is not None:
                        between()

            def turn_tiles(pair, half):
                for b in range(4 * half, 4 * half + 4):
                    n = 8 * pair + b
                    if b % 4 == 0:
                        for i in range(2):
                            if pair == 0:
                                pe.wait_ge(mem_landed[i][half], 16)
                            else:
                                pe.wait_ge(tile_scaled, 2 * (pair - 1) + i + 1)
                    if pair == 0 and b == 7:
                        pe.wait_ge(bank_taken, 1)
                    if n >= 12:
                        pe.wait_ge(bank_taken, n - 3)
                    for j in range(2):
                        kt = 2 * b + j
                        for i in range(2):
                            last = pe.transpose(turn_ps(pair, b)[:, 2 * P * j + P * i:2 * P * j + P * (i + 1)],
                                                stage[:, (2 * pair + i) % 4, P * kt:P * (kt + 1)], ident[:])
                    last.then_inc(bank_turned, 1)

            def turn_v(head_v, strip_v, blocks):
                pe.wait_ge(strip_free, strip_v + 1)
                if not isinstance(head_v, int) or head_v > 0:
                    pe.wait_ge(v_ready, head_v)
                for b in range(blocks):
                    last = pe.transpose(vt_ps[:, P * b:P * (b + 1)], vT[:, P * b:P * (b + 1)], ident[:])
                last.then_inc(v_turned, 1)

            def scores(head, blocks):
                pe.wait_ge(strip_free, (head.strip_q if head.memory else head.strip_k) + 1)
                for qb in blocks:
                    qs = (q[:, 0, P * qb:P * (qb + 1)], q[:, 1, P * qb:P * (qb + 1)])
                    if head.memory:
                        dst = score_ps[qb // 2][:, NMEM * (qb % 2):NMEM * (qb % 2 + 1)]
                        last = three(dst, qs, (kmv[:, 4 * head.m], kmv[:, 4 * head.m + 1]), True, True)
                        if qb % 2:
                            last.then_inc(scores_done, 1)
                    else:
                        n = P * (qb + 1)
                        dst = score_ps[qb % 2]
                        pe.matmul(dst[:, 0:n], qs[0], kv[:, 0:n], start=True, stop=False, skip_group_check=True)
                        pe.matmul(dst[:, 0:n], qs[1], kv[:, 0:n], start=False, stop=False, skip_group_check=True)
                        pe.matmul(dst[:, 0:n], qs[0], kv[:, S:S + n], start=False, stop=True,
                                  skip_group_check=True).then_inc(scores_done, 1)

            def turn_probs(head, groups):
                for g in groups:
                    if head.memory:
                        blocks = [(qb, kb) for kb in range(MB) for qb in (2 * g, 2 * g + 1)]
                        pe.wait_ge(prob_ready, head.scores + g + 1)
                    else:
                        blocks = [[(0, 0), (1, 0), (1, 1)], [(2, k) for k in range(3)], [(3, k) for k in range(4)]][g]
                        pe.wait_ge(prob_ready, head.scores + g + 2)
                        if g == 2:
                            pe.wait_ge(pt_ready, head.pt + 1)
                    for i, (qb, kb) in enumerate(blocks):
                        if head.memory:
                            src = prob[:, g, NMEM * (qb % 2) + P * kb:NMEM * (qb % 2) + P * (kb + 1)]
                        else:
                            src = prob[:, qb % 2, P * kb:P * (kb + 1)]
                        last = pe.transpose(pt_ps[g % 2][:, P * i:P * (i + 1)], src, ident[:])
                    last.then_inc(pt_turned, 1)

            def prob_times_v(head):
                pe.wait_ge(pt_ready, head.pt + (2 if head.memory else 3))
                pe.wait_ge(v_ready, head.v + 1)
                if not isinstance(head.hh, int) or head.hh > 0:
                    pe.wait_ge(y_raw, head.hh)
                else:
                    pe.wait_ge(f_z, 1)
                nb = MB if head.memory else QB
                for hl_v, hl_p in ((0, 0), (1, 0), (0, 1)):
                    for kb in range(nb):
                        first = 0 if head.memory else P * kb
                        if head.memory:
                            v = kmv[:, 4 * head.m + 2 + hl_v, P * kb:P * (kb + 1)]
                        else:
                            v = kv[:, S * (2 + hl_v) + P * kb:S * (2 + hl_v) + P * (kb + 1)]
                        last = pe.matmul(o_ps[:, first:S], v, pT[:, hl_p, kb, first:S],
                                         start=(hl_v, hl_p, kb) == (0, 0, 0), stop=(hl_p == 1 and kb == nb - 1),
                                         skip_group_check=True)
                last.then_inc(pv_done, 1)

            def make_tables():
                pe.wait_ge(mask_row_ready, 1)
                pe.wait_ge(rel_landed, 32)
                for bank, lo_, hi_ in table_banks:
                    pe.matmul(bank[0:NA, 0:hi_ - lo_], relT[:], hot[:, lo_:hi_], start=True, stop=True
                              ).then_inc(table_made, 1)

            pe.wait_ge(pool_consts, 1)
            for i in range(WARM_UP):
                pe.matmul(mem_ps[i % 4][:], waste[:, 0:P], waste[:, 0:S], start=True, stop=True)
            pe.wait_ge(pool_consts, 4)
            pe.wait_ge(gain_rows_landed, 32)
            for i in range(2):
                pe.transpose(strip_ps[0][:, KT * i:KT * (i + 1)], gain_rows[:, i], ident[0:KT, 0:KT]
                             ).then_inc(gain_turned, 1)
            turn_tiles(0, 0)
            turn_tiles(0, 1)

            def spread_rstd():
                pe.wait_ge(diag_ready, MB)
                pe.matmul(o_ps[:, 0:NMEM], ones[:], rstd_diag[:], start=True, stop=True).then_inc(rstd_spread, 1)

            def between(t):
                if t == 0:
                    pe.wait_ge(bank_taken, 8)
                if t == 1:
                    spread_rstd()
                if t in TURN_DURING:
                    turn_tiles(*TURN_DURING[t])

            pe.wait_ge(gain_copied, 1)
            pe.wait_ge(bank_taken, 4)
            for t in range(STRIPS_MEM):
                strip(t, t % 2, memT, NMEM, lambda: between(t))
                if t == 3:
                    make_tables()
                if t == STRIPS_MEM // 2 + 1:
                    pe.wait_ge(table_copied, 2)
                if t > STRIPS_MEM // 2:
                    turn_v(t - 1 - STRIPS_MEM // 2, t - 1, MB)
            pe.wait_ge(bank_taken, 8 * PAIRS)
            pe.wait_ge(wf_ready, 1)
            for kt in range(KT):
                for h in range(2):
                    last = pe.matmul(o_ps[:], wf[:, 64 * kt:64 * kt + P], xT[:, h, kt], start=kt + h == 0,
                                     stop=kt == KT - 1 and h == 1, skip_group_check=True)
            last.then_inc(f_done, 1)
            turn_v(NM - 1, STRIPS_MEM - 1, MB)

            for m in range(NM):
                head = MHead(m)
                strip(head.strip_q, 0, xT, S)
                if m:
                    turn_probs(MHead(m - 1), (0, 1))
                strip(head.strip_g, 1, xT, S)
                if m:
                    prob_times_v(MHead(m - 1))
                scores(head, range(QB))

            def head_strips(a, last_head):
                head = ABHead(a)
                strip(head.strip_q, 0, xT, S)
                turn_probs(last_head, (0, 1) if last_head.memory else (1, 2))
                strip(head.strip_k, 1, xT, S)
                prob_times_v(last_head)
                strip(head.strip_v, 0, xT, S)
                scores(head, (0, 1))
                strip(head.strip_g, 1, xT, S)
                turn_probs(head, (0,))
                scores(head, (2, 3))
                turn_v(head.v, head.strip_v, QB)

            head_strips(0, MHead(NM - 1))
            with pe.Fori(1, NAB) as a:
                head_strips(a, ABHead(a - 1))

            def out_piece(c, p, blocks, banks):
                e0 = out_e0(p)
                pe.wait_ge(lo_done, lo_count(PIECES + OPC * c + p)[1])
                for s, bank in zip(blocks, banks):
                    for j in range(2):
                        tok = slice(P * s, P * (s + 1))
                        w = wout_split[:, OUT_SLOT[p], :, S * j:S * (j + 1)]
                        last = three(bank[:], (y[:, 0, e0 + j, tok], y[:, 1, e0 + j, tok]), (w[:, 0], w[:, 1]),
                                     p == 0 and j == 0, p == OPC - 1 and j == 1)
                    if p == OPC - 1:
                        last.then_inc(o_done, 1)
                return last

            last_head = ABHead(NAB - 1)
            pe.wait_ge(strip_free, STRIPS - 1)
            pe.wait_ge(y_ready, NH - 1)
            for p in range(OPC):
                if p == OPC - 1:
                    pe.wait_ge(y_ready, NH)
                out_piece(0, p, (0,), strip_ps[0:1])
                if p == 0:
                    pe.wait_ge(strip_free, STRIPS)
                out_piece(0, p, (1,), strip_ps[1:2])
                if p == 1:
                    turn_probs(last_head, (1, 2))
                if p == 4:
                    prob_times_v(last_head)

            def out_second_pair(c):
                for p in range(OPC):
                    last = out_piece(c, p, (2, 3), score_ps)
                    if p < OPC - 1:
                        last.then_inc(out_used, 1)

            out_second_pair(0)
            with pe.Fori(1, OCH - 1) as c:
                pe.wait_ge(o_copied, QB * c - 2)
                for p in range(OPC):
                    out_piece(c, p, (0, 1), strip_ps)
                pe.wait_ge(o_copied, QB * c)
                out_second_pair(c)
            c = OCH - 1
            pe.wait_ge(o_copied, QB * c - 2)
            for p in range(OPC):
                out_piece(c, p, (0, 1), strip_ps)
            pe.wait_ge(o_copied, QB * c)
            for s in (2, 3):
                for p in range(OPC):
                    out_piece(c, p, (s,), (score_ps[s - 2],))

        def strip_piece(t, par, rnd, half):
            slot = 2 * par + half
            return 2 * t + half, slot, rnd, ring[:, slot]

        def out_split(c, p):
            return PIECES + OPC * c + p, p % RING, PIECES // RING + 2 * c + p // RING, wout_split[:, OUT_SLOT[p]]

        def strip_after(head, j):
            if head.memory:
                return (head.strip_g, 1, NM + head.m) if j == 0 else (head.strip_g + 1, 0, NM + head.m + 1)
            first = NM + NM + 2 * head.a
            return (head.strip_q + j + 1, (j + 1) % 2, first + (j + 1) // 2)

        def turned(bank, g, memory):
            if memory:
                return [(slice(0, S), slice(0, MB), slice(2 * P * g, 2 * P * (g + 1)))]
            return {0: [(slice(0, 2 * P), slice(0, 1), slice(0, 2 * P)), (slice(2 * P, 3 * P), slice(1, 2), slice(P, 2 * P))],
                    1: [(slice(0, 3 * P), slice(0, 3), slice(2 * P, 3 * P))],
                    2: [(slice(0, 4 * P), slice(0, 4), slice(3 * P, 4 * P))]}[g]

        def turned_dest(pair, h, kt):
            return memT[:, h, kt] if pair == 0 else xT[:, h, kt, 2 * P * (pair - 1):2 * P * pair]

        LATER = [(0, 1), (1, 2)]

        @block.scalar
        def _(act):
            def hi(piece, *gates):
                n, slot, rnd, dst = piece
                act.wait_ge(raw_landed[slot], 16 * (rnd + 1))
                for s_, v_ in gates:
                    act.wait_ge(s_, v_)
                act.activation(dst[:, 0], raw[:, slot], ACTF.Copy).then_inc(hi_done, 1)

            def hi_strip(ref, half):
                t = ref[0]
                piece = strip_piece(*ref, half)
                if isinstance(t, int) and t < 2:
                    hi(piece)
                else:
                    hi(piece, (piece_used, 2 * t + half - RING + 1))

            def hi_out(c, p):
                if isinstance(c, int) and c == 0:
                    hi(out_split(0, p), (piece_used, PIECES - 1 if p < OPC // 2 else PIECES))
                elif p < OPC - 1:
                    hi(out_split(c, p), (out_used, (OPC - 1) * (c - 1) + p + 1))
                else:
                    hi(out_split(c, p), (o_done, QB * c))

            def squares(t):
                if t >= MB:
                    act.wait_ge(stage_landed[t - MB], 16)
                    act.wait_ge(squares_done, t - 1)
                act.activation(waste[:], stage[:, t % 4], ACTF.Square, accum_out=sq[:, t:t + 1]
                               ).then_inc(squares_done, 1)

            def root(count, col, n=1, source=squares_done):
                act.wait_ge(source, count)
                act.activation(stat[:, 1, col:col + n], sq[:, col:col + n], ACTF.Sqrt, scale=1.0 / D, bias=eps[:]
                               ).then_inc(root_done, 1)

            def hi_tiles(pair, b0, b1):
                for b in range(b0, b1):
                    act.wait_ge(bank_turned, 8 * pair + b + 1)
                    for j in range(2):
                        kt = 2 * b + j
                        last = act.activation(turned_dest(pair, 0, kt), turn_ps(pair, b)[:, 2 * P * j:2 * P * (j + 1)],
                                              ACTF.Copy, scale=gains[:, min(pair, 1), kt:kt + 1])
                    last.then_inc(bank_hi, 1)

            def hi_y(head):
                act.wait_ge(y_raw, head.hh + 1)
                act.activation(y[:, 0, head.y_tile], ybuf[:], ACTF.Copy).then_inc(y_hi, 1)

            def tanh_gate(head):
                act.wait_ge(piece_used, 2 * head.strip_g + 2)
                if not isinstance(head.hh, int) or head.hh > 0:
                    act.wait_ge(y_raw, head.hh)
                act.activation(gate[:], strip_ps[1][:], ACTF.Tanh, scale=0.5).then_inc(gate_tanh, 1)

            def hi_q(head):
                act.wait_ge(piece_used, 2 * head.strip_q + 2)
                act.wait_ge(scores_done, head.scores)
                act.activation(q[:, 0], strip_ps[0][:], ACTF.Copy, scale=SCALE).then_inc(q_hi, 1)

            def hi_k(head):
                act.wait_ge(piece_used, 2 * head.strip_k + 2)
                act.activation(kv[:, 0:S], strip_ps[1][:], ACTF.Copy).then_inc(k_hi, 1)

            def hi_v(count, dst, n):
                act.wait_ge(v_turned, count + 1)
                act.activation(dst, vt_ps[:, 0:n], ACTF.Copy).then_inc(v_hi, 1)

            def exps(head, i):
                act.wait_ge(negmax_ready, head.scores + i + 1)
                if head.memory:
                    if head.m > 0:
                        act.wait_ge(pt_turned, head.pt - 1 + i)
                    for qb in (2 * i, 2 * i + 1):
                        cols = slice(NMEM * (qb % 2), NMEM * (qb % 2 + 1))
                        last = act.activation(prob[:, i, cols], score_ps[i][:, cols], ACTF.Exp,
                                              bias=negmax[:, qb:qb + 1], accum_out=rowsum[:, qb:qb + 1])
                else:
                    n = P * (i + 1)
                    last = act.activation(prob[:, i % 2, 0:n], prob[:, i % 2, 0:n], ACTF.Exp, scale=-1.0,
                                          bias=negmax[:, i:i + 1], accum_out=rowsum[:, i:i + 1])
                last.then_inc(exp_done, 1)

            def hi_pt(head, g):
                act.wait_ge(pt_turned, head.pt + g + 1)
                for src, kbs, qs in turned(None, g, head.memory):
                    last = act.activation(pT[:, 0, kbs, qs], pt_ps[g % 2][:, src].rearrange(
                        "p (k t) -> p k t", k=kbs.stop - kbs.start), ACTF.Copy)
                last.then_inc(pt_hi, 1)

            def while_q(last, split):
                tanh_gate(last)
                split(0)
                if last.memory:
                    exps(last, 0)
                    exps(last, 1)
                else:
                    exps(last, 2)
                    exps(last, 3)
                    hi_pt(last, 0)
                split(1)

            def while_k(head, last, split):
                if head is not None:
                    hi_q(head)
                split(0)
                if not last.memory:
                    hi_v(last.v, kv[:, 2 * S:3 * S], S)
                one, two = LATER[not last.memory]
                hi_pt(last, one)
                split(1)
                hi_pt(last, two)

            def while_v(head, last, split):
                if head is not None:
                    hi_k(head)
                split(0)
                hi_y(last)
                split(1)

            for half in range(2):
                cols = slice(D // 2 * half, D // 2 * (half + 1))
                act.dma_start(stage[:, 0, cols], token_tile(0)[:, cols]).then_inc(mem_landed[0][half], 16)
            act.wait_ge(pool_consts, 2)
            act.activation(stat[:, 1, 0:1], eps[:], ACTF.Sqrt)
            act.wait_ge(gain_copied, 1)
            hi_tiles(0, 0, 2)
            hi_strip((0, 0, 0), 0)
            hi_tiles(0, 2, 4)
            hi_tiles(0, 4, 6)
            hi_strip((0, 0, 0), 1)
            hi_tiles(0, 6, 8)
            for t in range(STRIPS_MEM):
                next_strip = (t + 1, (t + 1) % 2, (t + 1) // 2)
                hi_strip(next_strip, 0)
                if 1 <= t <= NM:
                    act.wait_ge(strip_free, t)
                    act.activation(kmv[:, 4 * (t - 1)], k_mem[:], ACTF.Copy
                                   ).then_inc(k_hi, 1)
                hi_strip(next_strip, 1)
                if t == 0:
                    for half in range(2):
                        act.wait_ge(mem_landed[0][half], 16)
                    squares(0)
                    act.wait_ge(mem_squared, 1)
                    root(1, 0, MB)
                if t >= 6:
                    hi_v(t - 6, kmv[:, 4 * (t - 6) + 2], NMEM)
                if t in TURN_DURING:
                    pair, half = TURN_DURING[t]
                    hi_tiles(pair, 4 * half, 4 * half + 4)
                if t in SQUARE_DURING:
                    squares(SQUARE_DURING[t])
                    root(SQUARE_DURING[t], SQUARE_DURING[t])
                if t == 5:
                    act.wait_ge(forget_landed, 32)
                    act.wait_ge(wf_cleared, 1)
                    act.activation(wf[:, 0:KT * 64].rearrange("p (k c) -> p k c", c=64)[:, :, 0:NB], wf_raw[:],
                                   ACTF.Copy).then_inc(wf_hi, 1)
            hi_v(2, kmv[:, 4 * 2 + 2], NMEM)

            for m in range(NM):
                head = MHead(m)
                if m >= 2:
                    hi_y(MHead(m - 2))
                if m == 0:
                    act.wait_ge(f_done, 1)
                    act.activation(fbuf[:, 1], o_ps[32:32 + NB, :], ACTF.Copy).then_inc(f_low, 1)
                    hi_strip(strip_after(head, 0), 0)
                    hi_v(3, kmv[:, 4 * 3 + 2], NMEM)
                    hi_strip(strip_after(head, 0), 1)
                else:
                    while_q(MHead(m - 1), lambda half: hi_strip(strip_after(head, 0), half))
                hi_q(head)
                hi_strip(strip_after(head, 1), 0)
                if m:
                    hi_pt(MHead(m - 1), 0)
                    hi_pt(MHead(m - 1), 1)
                else:
                    act.wait_ge(f_neg, 1)
                    act.activation(fbuf[:, 1], fbuf[:, 2], ACTF.Exp).then_inc(f_exp, 1)
                hi_strip(strip_after(head, 1), 1)

            def head_strips(a, last):
                head = ABHead(a)
                if last.memory:
                    hi_y(MHead(last.m - 1))
                while_q(last, lambda half: hi_strip(strip_after(head, 0), half))
                while_k(head, last, lambda half: hi_strip(strip_after(head, 1), half))
                while_v(head, last, lambda half: hi_strip(strip_after(head, 2), half))
                final = isinstance(a, int) and a == NAB - 1
                if not final:
                    hi_strip(strip_after(head, 3), 0)
                exps(head, 0)
                exps(head, 1)
                if not final:
                    hi_strip(strip_after(head, 3), 1)
                else:
                    hi_out(0, 0)
                    hi_out(0, 1)

            head_strips(0, MHead(NM - 1))
            with act.Fori(1, NAB - 1) as a:
                head_strips(a, ABHead(a - 1))
            head_strips(NAB - 1, ABHead(NAB - 2))
            last_head = ABHead(NAB - 1)
            while_q(last_head, lambda half: hi_out(0, 2 + half))
            while_k(None, last_head, lambda half: hi_out(0, 4 + half))
            while_v(None, last_head, lambda half: hi_out(0, 6 + half))

            def copy_out(c, s):
                act.wait_ge(o_done, QB * c + s + 1)
                bank = (strip_ps + score_ps)[s]
                act.activation(waste_o[:, s], bank[:], ACTF.Square, accum_out=part[:, s:s + 1]
                               ).then_inc(part_done, 1)
                act.activation(o_sb[:, s, bass.ds(c * S, S)], bank[:], ACTF.Copy).then_inc(o_copied, 1)

            with act.Fori(0, OCH - 1) as c:
                copy_out(c, 0)
                copy_out(c, 1)
                for p in range(OPC):
                    hi_out(c + 1, p)
                copy_out(c, 2)
                copy_out(c, 3)
            for s in range(QB):
                copy_out(OCH - 1, s)
                root(QB * (OCH - 1) + s + 1, s, source=ssq_done)

        @block.vector
        def _(dve):
            steps = [0]

            def chain(ins):
                steps[0] += 1
                ins.then_inc(stat_step, 1)
                dve.wait_ge(stat_step, steps[0])

            def minus(dst, a_, hi_):
                return dve.tensor_tensor(dst, a_, hi_.bitcast(F32), ALU.subtract)

            def lo(piece):
                n, slot, rnd, dst = piece
                if isinstance(n, int) and lo_count(n)[0]:
                    return
                dve.wait_ge(hi_done, n + 1)
                minus(dst[:, 1], raw[:, slot], dst[:, 0]).then_inc(lo_done, 1)

            def lo_strip(ref, half):
                lo(strip_piece(*ref, half))

            def rstd(count, col, meanwhile=lambda: None, n=1):
                c = slice(col, col + n)
                dve.tensor_scalar(stat[:, 0, c], sq[:, c], 1.0 / D, EPS, ALU.mult, ALU.add)
                meanwhile()
                dve.wait_ge(root_done, count)
                chain(dve.reciprocal(stat[:, 2, c], stat[:, 1, c]))
                if n == 1:
                    chain(dve.scalar_tensor_tensor(out=stat[:, 3, c], in0=stat[:, 2, c], scalar=stat[:, 2, c],
                                                   in1=stat[:, 0, c], op0=ALU.mult, op1=ALU.mult))
                else:
                    chain(dve.tensor_tensor(stat[:, 3, c], stat[:, 2, c], stat[:, 2, c], ALU.mult))
                    chain(dve.tensor_tensor(stat[:, 3, c], stat[:, 3, c], stat[:, 0, c], ALU.mult))
                chain(dve.tensor_scalar(stat[:, 3, c], stat[:, 3, c], -0.5, 1.5, ALU.mult, ALU.add))
                chain(dve.tensor_tensor(stat[:, 4, c], stat[:, 2, c], stat[:, 3, c], ALU.mult))

            def scale_tile(t):
                dve.wait_ge(squares_done, t)
                rstd(t, t)
                one = stage[:, t % 4]
                dve.tensor_scalar(one, one, stat[:, 4, t:t + 1], None, ALU.mult).then_inc(tile_scaled, 1)

            def lo_tiles(pair, half):
                for b in range(4 * half, 4 * half + 4):
                    dve.wait_ge(bank_hi, 8 * pair + b + 1)
                    for j in range(2):
                        kt = 2 * b + j
                        last = dve.scalar_tensor_tensor(
                            out=turned_dest(pair, 1, kt), in0=turn_ps(pair, b)[:, 2 * P * j:2 * P * (j + 1)],
                            scalar=gains[:, min(pair, 1), kt:kt + 1], in1=turned_dest(pair, 0, kt).bitcast(F32),
                            op0=ALU.mult, op1=ALU.subtract)
                    last.then_inc(bank_taken, 1)

            def gated(head):
                dve.wait_ge(pv_done, head.hh + 1)
                dve.wait_ge(strip_free, head.strip_g + 1)
                dve.scalar_tensor_tensor(out=ybuf[:], in0=o_ps[:], scalar=0.5, in1=gate[:], op0=ALU.mult,
                                         op1=ALU.mult).then_inc(y_raw, 1)

            def lo_y(head):
                dve.wait_ge(y_hi, head.hh + 1)
                minus(y[:, 1, head.y_tile], ybuf[:], y[:, 0, head.y_tile]).then_inc(y_ready, 1)

            def silu_gate(head):
                dve.wait_ge(gate_tanh, head.hh + 1)
                dve.scalar_tensor_tensor(out=gate[:], in0=gate[:], scalar=1.0, in1=strip_ps[1][:], op0=ALU.add,
                                         op1=ALU.mult).then_inc(strip_free, 1)

            def lo_q(head):
                dve.wait_ge(q_hi, head.hh + 1)
                dve.scalar_tensor_tensor(out=q[:, 1], in0=strip_ps[0][:], scalar=SCALE, in1=q[:, 0].bitcast(F32),
                                         op0=ALU.mult, op1=ALU.subtract).then_inc(strip_free, 1)

            def lo_k(head):
                dve.wait_ge(k_hi, NM + head.a + 1)
                minus(kv[:, S:2 * S], strip_ps[1][:], kv[:, 0:S]).then_inc(strip_free, 1)

            def copy_v(strip_v, par):
                dve.wait_ge(piece_used, 2 * strip_v + 2)
                if isinstance(strip_v, int) and strip_v < STRIPS_MEM:
                    dve.tensor_tensor(vT[:, 0:NMEM], strip_ps[par][:, 0:NMEM], rstd_mem[:], ALU.mult
                                      ).then_inc(strip_free, 1)
                else:
                    dve.tensor_copy(vT[:], strip_ps[par][:]).then_inc(strip_free, 1)

            def lo_v(count, lo_, hi_, n):
                dve.wait_ge(v_hi, count + 1)
                minus(lo_, vt_ps[:, 0:n], hi_).then_inc(v_ready, 1)

            def row_max(head, i, forgetting=False):
                dve.wait_ge(scores_done, head.scores + i + 1)
                if head.memory:
                    two = slice(2 * i, 2 * i + 2)
                    dve.tensor_reduce(rowmax[:, two], score_ps[i][:].rearrange("p (a n) -> p a n", a=2), AX_X,
                                      ALU.max).then_inc(max_done, 1)
                    dve.wait_ge(max_done, 2 * head.m + i + 1)
                    dve.tensor_scalar(negmax[:, two], rowmax[:, two], -1.0, None, ALU.mult).then_inc(negmax_ready, 1)
                    return
                n = P * (i + 1)
                if i == 0 and forgetting:
                    dve.wait_ge(bias_masked, MASK_PARTS * (head.a - NA + 1))
                elif i == 0:
                    dve.wait_ge(bias_landed, 16 * (head.a + 1))
                dve.wait_ge(pt_turned, head.pt + (i >= 2))
                if not isinstance(head.a, int):
                    dve.memset(pace[:, i:i + 1], 0.0)
                if forgetting:
                    b = bias_low[:, LOW_AT[i]:LOW_AT[i] + n] if i < QB - 1 else bias[:]
                else:
                    b = bias[:, S - n:S]
                dve.tensor_tensor_reduce(prob[:, i % 2, 0:n], score_ps[i % 2][:, 0:n], b, -1.0, BIG, ALU.add,
                                         ALU.min, negmax[:, i:i + 1]).then_inc(negmax_ready, 1)

            def normalise(head, pair):
                dve.wait_ge(exp_done, head.scores + (pair + 1 if head.memory else 2 * pair + 2))
                two = slice(2 * pair, 2 * pair + 2)
                dve.reciprocal(rinv[:, two], rowsum[:, two]).then_inc(rinv_ready, 1)
                dve.wait_ge(rinv_ready, 2 * head.hh + pair + 1)
                for qb in (2 * pair, 2 * pair + 1):
                    if head.memory:
                        part = prob[:, pair, NMEM * (qb % 2):NMEM * (qb % 2 + 1)]
                    else:
                        part = prob[:, qb % 2, 0:P * (qb + 1)]
                    last = dve.tensor_scalar(part, part, rinv[:, qb:qb + 1], None, ALU.mult)
                    if not head.memory:
                        last.then_inc(prob_ready, 1)
                if head.memory:
                    last.then_inc(prob_ready, 1)

            def lo_pt(head, g):
                dve.wait_ge(pt_hi, head.pt + g + 1)
                for src, kbs, qs in turned(None, g, head.memory):
                    last = minus(pT[:, 1, kbs, qs], pt_ps[g % 2][:, src].rearrange(
                        "p (k t) -> p k t", k=kbs.stop - kbs.start), pT[:, 0, kbs, qs])
                last.then_inc(pt_ready, 1)

            def while_q(last, split, forgetting=False):
                if last.memory:
                    row_max(last, 0)
                    row_max(last, 1)
                else:
                    row_max(last, 2, forgetting)
                    row_max(last, 3, forgetting)
                silu_gate(last)
                split(0)
                if last.memory:
                    normalise(last, 0)
                    normalise(last, 1)
                else:
                    normalise(last, 1)
                    lo_pt(last, 0)
                split(1)

            def while_k(head, last, split):
                if head is not None:
                    lo_q(head)
                split(0)
                if not last.memory:
                    lo_v(last.v, kv[:, 3 * S:4 * S], kv[:, 2 * S:3 * S], S)
                one, two = LATER[not last.memory]
                lo_pt(last, one)
                split(1)
                lo_pt(last, two)

            def while_v(head, last, split):
                if head is not None:
                    lo_k(head)
                gated(last)
                split(0)
                lo_y(last)
                split(1)

            dve.memset(relT[BUCKETS:BUCKETS + 1, :], 1.0).then_inc(mask_row_ready, 1)
            dve.wait_ge(gain_turned, 2)
            dve.tensor_copy(gains[:].rearrange("p g k -> p (g k)"), strip_ps[0][:, 0:2 * KT]).then_inc(gain_copied, 1)
            lo_tiles(0, 0)
            lo_strip((0, 0, 0), 0)
            lo_strip((0, 0, 0), 1)
            lo_tiles(0, 1)
            for t in range(STRIPS_MEM):
                if t == 1:
                    dve.wait_ge(rstd_spread, 1)
                    chain(dve.tensor_copy(rstd_mem[:], o_ps[:, 0:NMEM]))
                if 1 <= t <= NM:
                    dve.wait_ge(piece_used, 2 * t)
                    if t > 1:
                        dve.wait_ge(k_taken, t - 1)
                    dve.tensor_tensor(k_mem[:], strip_ps[(t - 1) % 2][:, 0:NMEM], rstd_mem[:], ALU.mult
                                      ).then_inc(strip_free, 1)
                if t in SCALE_DURING:
                    scale_tile(SCALE_DURING[t])
                if 1 <= t <= NM:
                    dve.wait_ge(k_hi, t)
                    minus(kmv[:, 4 * (t - 1) + 1], k_mem[:], kmv[:, 4 * (t - 1)]).then_inc(k_taken, 1)
                if t > NM:
                    if t > NM + 1:
                        dve.wait_ge(v_turned, t - 1 - NM)
                    copy_v(t - 1, (t - 1) % 2)
                for half in range(2):
                    lo_strip((t + 1, (t + 1) % 2, (t + 1) // 2), half)
                if t == STRIPS_MEM // 2 + 1:
                    for i, (bank, lo_, hi_) in enumerate(table_banks):
                        dve.wait_ge(table_made, i + 1)
                        dve.tensor_copy(table[:, lo_:hi_], bank[0:NA, 0:hi_ - lo_]).then_inc(table_copied, 1)
                if t >= 6:
                    lo_v(t - 6, kmv[:, 4 * (t - 6) + 3], kmv[:, 4 * (t - 6) + 2], NMEM)
                if t == 0:
                    for half in range(2):
                        dve.wait_ge(mem_landed[1][half], 16)
                    dve.tensor_tensor_reduce(waste_mem[:], stage[:, 1], stage[:, 1], 1.0, 0.0, ALU.mult, ALU.add,
                                             sq[:, 1:2]).then_inc(mem_squared, 1)
                    dve.wait_ge(mem_squared, 1)
                    dve.wait_ge(squares_done, 1)
                    rstd(1, 0, n=MB)
                    for i in range(MB):
                        dve.tensor_scalar(rstd_diag[:, i], ident[:], stat[:, 4, i:i + 1], None, ALU.mult
                                          ).then_inc(diag_ready, 1)
                if t in TURN_DURING:
                    lo_tiles(*TURN_DURING[t])
                if t == 5:
                    dve.memset(wf[:].bitcast(F32), 0.0).then_inc(wf_cleared, 1)
                    dve.wait_ge(wf_hi, 1)
                    wf_v = wf[:, 0:KT * 64].rearrange("p (k c) -> p k c", c=64)
                    minus(wf_v[:, :, 32:32 + NB], wf_raw[:], wf_v[:, :, 0:NB]).then_inc(wf_ready, 1)
            dve.wait_ge(v_turned, NM - 1)
            copy_v(STRIPS_MEM - 1, 1)
            lo_v(2, kmv[:, 4 * 2 + 3], kmv[:, 4 * 2 + 2], NMEM)

            for m in range(NM):
                head = MHead(m)
                if m >= 2:
                    gated(MHead(m - 2))
                    lo_y(MHead(m - 2))
                if m == 0:
                    dve.wait_ge(f_low, 1)
                    dve.scalar_tensor_tensor(out=fbuf[:, 0], in0=o_ps[0:NB, :], scalar=bfor[:, 0:1], in1=fbuf[:, 1],
                                             op0=ALU.add, op1=ALU.add).then_inc(f_z, 1)
                    lo_strip(strip_after(head, 0), 0)
                    lo_v(3, kmv[:, 4 * 3 + 3], kmv[:, 4 * 3 + 2], NMEM)
                    lo_strip(strip_after(head, 0), 1)
                else:
                    while_q(MHead(m - 1), lambda half: lo_strip(strip_after(head, 0), half))
                lo_q(head)
                lo_strip(strip_after(head, 1), 0)
                if m:
                    lo_pt(MHead(m - 1), 0)
                    lo_pt(MHead(m - 1), 1)
                lo_strip(strip_after(head, 1), 1)
                if m == 1:
                    dve.wait_ge(f_den, 1)
                    dve.reciprocal(fbuf[:, 3], fbuf[:, 3]).then_inc(f_rec, 1)

            def head_strips(a, last, last_forgets, forgets):
                head = ABHead(a)
                if last.memory:
                    gated(MHead(last.m - 1))
                    lo_y(MHead(last.m - 1))
                while_q(last, lambda half: lo_strip(strip_after(head, 0), half), last_forgets)
                while_k(head, last, lambda half: lo_strip(strip_after(head, 1), half))
                while_v(head, last, lambda half: lo_strip(strip_after(head, 2), half))
                final = isinstance(a, int) and a == NAB - 1
                row_max(head, 0, forgets)
                row_max(head, 1, forgets)
                dve.wait_ge(v_turned, head.v)
                copy_v(head.strip_v, 0)
                if not final:
                    lo_strip(strip_after(head, 3), 0)
                normalise(head, 0)
                if not final:
                    lo_strip(strip_after(head, 3), 1)
                else:
                    lo(out_split(0, 0))
                    lo(out_split(0, 1))

            head_strips(0, MHead(NM - 1), False, False)
            dve.wait_ge(f_parts, 1)
            dve.tensor_tensor_scan(fbuf[:, 1], fbuf[:, 3], fbuf[:, 0], 0.0, ALU.add, ALU.add).then_inc(f_scan, 1)
            with dve.Fori(1, NA) as a:
                head_strips(a, ABHead(a - 1), False, False)
            head_strips(NA, ABHead(NA - 1), False, True)
            with dve.Fori(NA + 1, NAB - 1) as a:
                head_strips(a, ABHead(a - 1), True, True)
            head_strips(NAB - 1, ABHead(NAB - 2), True, True)
            last_head = ABHead(NAB - 1)
            while_q(last_head, lambda half: lo(out_split(0, 2 + half)), True)
            while_k(None, last_head, lambda half: lo(out_split(0, 4 + half)))
            while_v(None, last_head, lambda half: lo(out_split(0, 6 + half)))

            def add_squares(c, s):
                dve.wait_ge(part_done, QB * c + s + 1)
                one = slice(s, s + 1)
                return dve.tensor_tensor(sq[:, one], sq[:, one], part[:, one], ALU.add)

            def gain_out(c, s):
                dve.wait_ge(o_copied, QB * c + s + 1)
                o = o_sb[:, s, bass.ds(c * S, S)]
                dve.tensor_tensor(o, o, gpost[:, bass.ds(c * S, S)], ALU.mult).then_inc(o_gained, 1)

            chain(dve.memset(sq[:], 0.0))
            dve.wait_ge(gpost_landed, 16)
            with dve.Fori(0, OCH - 1) as c:
                for s in range(QB):
                    if s == 2:
                        for p in range(OPC):
                            lo(out_split(c + 1, p))
                    add_squares(c, s).then_inc(ssq_done, 1)
                    gain_out(c, s)
            for s in range(QB):
                dve.wait_ge(ssq_done, QB * (OCH - 2) + s + 1)
                add_squares(OCH - 1, s).then_inc(ssq_done, 1)
                dve.wait_ge(ssq_done, QB * (OCH - 1) + s + 1)
                rstd(TILES + s, s, lambda: gain_out(OCH - 1, s))
                dve.wait_ge(xres_landed[s % 2], 16 * (s // 2 + 1))
                for j in range(4):
                    if j == 3:
                        dve.wait_ge(o_gained, QB * (OCH - 1) + s + 1)
                    cols = slice(S * j, S * (j + 1))
                    dve.scalar_tensor_tensor(out=o_sb[:, s, cols], in0=o_sb[:, s, cols], scalar=stat[:, 4, s:s + 1],
                                             in1=xres[:, s % 2, cols], op0=ALU.mult, op1=ALU.add
                                             ).then_inc(final_done, 1)

        @block.gpsimd
        def _(pool):
            pool.memset(waste[:, 0:S], 0.0).then_inc(pool_consts, 1)
            pool.memset(ident[:], 0.0).then_inc(f_pool, 1)
            pool.memset(eps[:], EPS).then_inc(pool_consts, 1)
            pool.memset(ones[:], 1.0).then_inc(pool_consts, 1)
            pool.memset(mask[:], 0.0).then_inc(f_pool, 1)
            pool.wait_ge(f_pool, 2)
            pool.affine_select(out=ident[:], in_=ident[:], compare_op=ALU.not_equal, fill=1.0, base=0,
                               pattern=[[-1, P]], channel_multiplier=1).then_inc(pool_consts, 1)
            pool.affine_select(out=mask[:], in_=mask[:], compare_op=ALU.is_ge, fill=NEG, base=0,
                               pattern=[[-1, P]], channel_multiplier=1).then_inc(pool_consts, 1)

            def lo(n):
                _, slot, _, dst = strip_piece(n // 2, n // 2 % 2, n // 4, n % 2)
                pool.wait_ge(hi_done, n + 1)
                pool.tensor_tensor(dst[:, 1], raw[:, slot], dst[:, 0].bitcast(F32), ALU.subtract).then_inc(lo_pool, 1)

            for n in POOL_PIECES:
                lo(n)

            steps = [2]

            def chain(ins):
                steps[0] += 1
                ins.then_inc(f_pool, 1)
                pool.wait_ge(f_pool, steps[0])

            z, e, s2, p = fbuf[:, 0], fbuf[:, 1], fbuf[:, 2], fbuf[:, 3]
            pool.wait_ge(f_z, 1)
            chain(pool.tensor_scalar(s2, z, 0.0, 2.0, ALU.min, ALU.mult))
            pool.tensor_tensor(s2, s2, z, ALU.subtract).then_inc(f_neg, 1)
            chain(pool.tensor_scalar(z, z, 0.0, None, ALU.min))
            pool.wait_ge(f_exp, 1)
            pool.tensor_scalar(p, e, 2.0, None, ALU.add).then_inc(f_den, 1)
            pool.wait_ge(f_rec, 1)
            chain(pool.tensor_tensor(e, e, p, ALU.mult))
            chain(pool.tensor_tensor(s2, e, e, ALU.mult))
            chain(pool.tensor_scalar(p, s2, SERIES[0], None, ALU.mult))
            for c in SERIES[1:]:
                chain(pool.tensor_scalar(p, p, c, None, ALU.add))
                chain(pool.tensor_tensor(p, p, s2, ALU.mult))
            chain(pool.tensor_scalar(p, p, 1.0, None, ALU.add))
            chain(pool.tensor_tensor(p, p, e, ALU.mult))
            pool.tensor_tensor(z, p, z, ALU.subtract).then_inc(f_parts, 1)

            with pool.Fori(NA, NAB) as a:
                pool.wait_ge(bias_landed, 16 * (a + 1))
                pool.tensor_tensor(bias[:, S - P:S], bias[:, S - P:S], mask[:], ALU.add).then_inc(bias_masked, 1)
                for i in range(QB - 1):
                    diagonal = slice(LOW_AT[i] + P * i, LOW_AT[i] + P * (i + 1))
                    pool.tensor_tensor(bias_low[:, diagonal], bias[:, P * i:P * (i + 1)], mask[:], ALU.add
                                       ).then_inc(bias_masked, 1)
                for i in range(1, QB - 1):
                    pool.tensor_copy(bias_low[:, LOW_AT[i]:LOW_AT[i] + P * i], bias[:, 0:P * i]
                                     ).then_inc(bias_masked, 1)


_INS = ["x", "mem", "w_in", "b_forget", "w_mem_kv", "w_out", "g_pre", "g_post", "g_mem", "rel_bias"]


def kernel(**inputs):
    import numpy as _np
    import concourse.bacc as _bacc
    from concourse import mybir as _mybir
    from concourse.bass_utils import run_bass_kernel_spmd as _run

    nc = _bacc.Bacc("TRN2", target_bir_lowering=False, num_devices=1, dynamic_dma_scratch_size=1024)
    arrays, args = {}, []
    for name in _INS + ["buckets"]:
        a = bucket_rows() if name == "buckets" else _np.ascontiguousarray(inputs[name])
        arrays[f"in_{name}_dram"] = a
        args.append(nc.dram_tensor(f"in_{name}_dram", a.shape, _mybir.dt.from_np(a.dtype), kind="ExternalInput").ap())
    args.append(nc.dram_tensor("out_dram", (1, S, D), _mybir.dt.float32, kind="ExternalOutput").ap())
    build(nc, *args)
    r = _run(nc, [arrays], core_ids=[0])
    return r.results[0]["out_dram"]
```
